# Optimizing a Trainium2 kernel written in Bass

```python
import jax, jax.numpy as jnp
from jax import lax
import numpy as np

D_MODEL = 1024
BATCH = 1
SEQ = 1024
DEPTH = 1
DEC_BATCH = 8
DEC_SEQ = 1
PAST_LEN = 8192
PAGE_SIZE = 128

D_MIX = 2 * D_MODEL
D_LRU = D_MIX // 2
D_SSD = D_MIX - D_LRU
LRU_HEADS = 16
LRU_BS = D_LRU // LRU_HEADS
LRU_C = 8.0
SSD_HEAD_DIM = 64
SSD_HEADS = D_SSD // SSD_HEAD_DIM
SSD_GROUPS = 2
SSD_STATE = 128
SSD_CHUNK = 128
D_XBC = D_SSD + 2 * SSD_GROUPS * SSD_STATE
CONV_W = 4
D_FF = 256 * ((8 * D_MODEL // 3 + 255) // 256)
D_IN = 2 * D_LRU + D_SSD + D_XBC + SSD_HEADS
EPS = 1e-6

kernel_name = "hymba_rglru_ssd_macaron_step"

def rmsnorm(x, g):
    xf = x.astype(jnp.float32)
    y = xf * lax.rsqrt(jnp.mean(xf * xf, axis=-1, keepdims=True) + EPS)
    return (y * g.astype(jnp.float32)).astype(x.dtype)

def swiglu(x, w_gate, w_up, w_down):
    return (jax.nn.silu(x @ w_gate) * (x @ w_up)) @ w_down

def causal_conv(x, buf, w, b):
    L = x.shape[1]
    ext = jnp.concatenate([buf.astype(x.dtype), x], axis=1)
    y = b
    for k in range(CONV_W):
        y = y + ext[:, k:k + L] * w[k]
    return y, ext[:, L:]

def _lin_combine(left, right):
    a_l, b_l = left
    a_r, b_r = right
    return a_l * a_r, a_r * b_l + b_r

def rg_lru(x, h0, gate_a_w, gate_a_b, gate_x_w, gate_x_b, lam):
    B, L, _ = x.shape
    f32 = jnp.float32
    xf = x.astype(f32)
    xb = xf.reshape(B, L, LRU_HEADS, LRU_BS)
    r = jax.nn.sigmoid(jnp.einsum('blhi,hij->blhj', xb, gate_a_w.astype(f32)).reshape(B, L, D_LRU) + gate_a_b.astype(f32))
    ig = jax.nn.sigmoid(jnp.einsum('blhi,hij->blhj', xb, gate_x_w.astype(f32)).reshape(B, L, D_LRU) + gate_x_b.astype(f32))
    log_a = -LRU_C * r * jax.nn.softplus(-lam.astype(f32))
    a = jnp.exp(log_a)
    u = jnp.sqrt(-jnp.expm1(2.0 * log_a)) * (ig * xf)
    u = u.at[:, 0].add(a[:, 0] * h0.astype(f32))
    _, h = lax.associative_scan(_lin_combine, (a, u), axis=1)
    return h, h[:, -1]

def ssd_scan(x, dt, A, Bm, Cm, h0):
    B, L, H, P = x.shape
    G, N = Bm.shape[2], Bm.shape[3]
    E = H // G
    Q = SSD_CHUNK if L >= SSD_CHUNK else L
    pad = (-L) % Q
    if pad:
        def _p(t):
            return jnp.pad(t, ((0, 0), (0, pad)) + ((0, 0),) * (t.ndim - 2))
        x, dt, Bm, Cm = _p(x), _p(dt), _p(Bm), _p(Cm)
    Lp = L + pad
    nc = Lp // Q
    xc = x.reshape(B, nc, Q, G, E, P)
    dtc = dt.reshape(B, nc, Q, G, E)
    Bc = Bm.reshape(B, nc, Q, G, N)
    Cc = Cm.reshape(B, nc, Q, G, N)
    Acs = jnp.cumsum(dtc * A.reshape(G, E), axis=2)
    seg = Acs[:, :, :, None] - Acs[:, :, None, :]
    causal = jnp.tril(jnp.ones((Q, Q), dtype=bool))[:, :, None, None]
    Lmat = jnp.exp(jnp.where(causal, seg, -jnp.inf))
    xdt = xc * dtc[..., None]
    CB = jnp.einsum('bcign,bcjgn->bcijg', Cc, Bc)
    y_diag = jnp.einsum('bcijg,bcijge,bcjgep->bcigep', CB, Lmat, xdt)
    decay_s = jnp.exp(Acs[:, :, -1:] - Acs)
    states = jnp.einsum('bcjgn,bcjge,bcjgep->bcgepn', Bc, decay_s, xdt)
    chunk_decay = jnp.exp(Acs[:, :, -1])

    def step(h, inp):
        st, dec = inp
        return h * dec[..., None, None] + st, h

    hT, h_prev = lax.scan(step, h0.reshape(B, G, E, P, N),
                          (jnp.moveaxis(states, 1, 0), jnp.moveaxis(chunk_decay, 1, 0)))
    h_prev = jnp.moveaxis(h_prev, 0, 1)
    y_off = jnp.einsum('bcign,bcige,bcgepn->bcigep', Cc, jnp.exp(Acs), h_prev)
    y = (y_diag + y_off).reshape(B, Lp, H, P)[:, :L]
    return y, hT.reshape(B, H, P, N)

def run_layer(x, lru_conv_buf, lru_h0, ssd_conv_buf, ssd_h0,
              ffn1_norm, ffn1_w_gate, ffn1_w_up, ffn1_w_down, mix_norm, w_in,
              lru_conv_w, lru_conv_b, lru_gate_a_w, lru_gate_a_b, lru_gate_x_w, lru_gate_x_b,
              lru_lambda, lru_out_norm, ssd_conv_w, ssd_conv_b, ssd_dt_bias, ssd_a_log, ssd_d,
              ssd_norm, w_out, ffn2_norm, ffn2_w_gate, ffn2_w_up, ffn2_w_down):
    B, L, _ = x.shape
    f32 = jnp.float32
    x = x + 0.5 * swiglu(rmsnorm(x, ffn1_norm), ffn1_w_gate, ffn1_w_up, ffn1_w_down)
    u = rmsnorm(x, mix_norm)
    proj = u @ w_in
    o1 = D_LRU
    o2 = 2 * D_LRU
    o3 = o2 + D_SSD
    o4 = o3 + D_XBC
    lru_x, lru_y, ssd_z, ssd_xbc, ssd_dt = jnp.split(proj, [o1, o2, o3, o4], axis=-1)
    lru_xc, new_lru_conv = causal_conv(lru_x, lru_conv_buf, lru_conv_w, lru_conv_b)
    h, lru_hT = rg_lru(lru_xc, lru_h0, lru_gate_a_w, lru_gate_a_b, lru_gate_x_w, lru_gate_x_b, lru_lambda)
    lru_out = rmsnorm(h * jax.nn.gelu(lru_y.astype(f32)), lru_out_norm).astype(x.dtype)
    xbc_c, new_ssd_conv = causal_conv(ssd_xbc, ssd_conv_buf, ssd_conv_w, ssd_conv_b)
    xbc_c = jax.nn.silu(xbc_c).astype(f32)
    xs, Bm, Cm = jnp.split(xbc_c, [D_SSD, D_SSD + SSD_GROUPS * SSD_STATE], axis=-1)
    xs = xs.reshape(B, L, SSD_HEADS, SSD_HEAD_DIM)
    Bm = Bm.reshape(B, L, SSD_GROUPS, SSD_STATE)
    Cm = Cm.reshape(B, L, SSD_GROUPS, SSD_STATE)
    dt = jax.nn.softplus(ssd_dt.astype(f32) + ssd_dt_bias.astype(f32))
    A = -jnp.exp(ssd_a_log.astype(f32))
    y, ssd_hT = ssd_scan(xs, dt, A, Bm, Cm, ssd_h0.astype(f32))
    y = (y + ssd_d.astype(f32)[:, None] * xs).reshape(B, L, D_SSD)
    gated = (y * jax.nn.silu(ssd_z.astype(f32))).reshape(B, L, SSD_GROUPS, D_SSD // SSD_GROUPS)
    ssd_out = rmsnorm(gated, ssd_norm.reshape(SSD_GROUPS, D_SSD // SSD_GROUPS)).reshape(B, L, D_SSD).astype(x.dtype)
    x = x + jnp.concatenate([lru_out, ssd_out], axis=-1) @ w_out
    x = x + 0.5 * swiglu(rmsnorm(x, ffn2_norm), ffn2_w_gate, ffn2_w_up, ffn2_w_down)
    return x, (new_lru_conv, lru_hT, new_ssd_conv, ssd_hT)

def setup_inputs(seed: int = 0) -> dict:
    key = jax.random.key(seed)
    ks = iter(jax.random.split(key, 40))

    def nrm(shape, scale):
        return jax.random.normal(next(ks), shape, jnp.float32) * scale

    def gain(shape):
        return 1.0 + nrm(shape, 0.05)

    lam_u = jax.random.uniform(next(ks), (DEPTH, D_LRU), jnp.float32, 0.9, 0.999)
    base = lam_u ** (1.0 / LRU_C)
    lru_lambda = jnp.log(base) - jnp.log1p(-base)
    dt0 = jnp.exp(jax.random.uniform(next(ks), (DEPTH, SSD_HEADS), jnp.float32, np.log(1e-3), np.log(1e-1)))
    ssd_dt_bias = dt0 + jnp.log(-jnp.expm1(-dt0))
    ssd_a_log = jnp.log(jax.random.uniform(next(ks), (DEPTH, SSD_HEADS), jnp.float32, 1.0, 16.0))
    return {
        "x_prompt": nrm((BATCH, SEQ, D_MODEL), 1.0),
        "x_sample": nrm((DEC_BATCH, DEC_SEQ, D_MODEL), 1.0),
        "state_lru_conv": nrm((DEPTH, DEC_BATCH, CONV_W - 1, D_LRU), 1.0),
        "state_lru_h": nrm((DEPTH, DEC_BATCH, D_LRU), 0.5),
        "state_ssd_conv": nrm((DEPTH, DEC_BATCH, CONV_W - 1, D_XBC), 1.0),
        "state_ssd_h": nrm((DEPTH, DEC_BATCH, SSD_HEADS, SSD_HEAD_DIM, SSD_STATE), 0.1),
        "ffn1_norm": gain((DEPTH, D_MODEL)),
        "ffn1_w_gate": nrm((DEPTH, D_MODEL, D_FF), D_MODEL ** -0.5),
        "ffn1_w_up": nrm((DEPTH, D_MODEL, D_FF), D_MODEL ** -0.5),
        "ffn1_w_down": nrm((DEPTH, D_FF, D_MODEL), D_FF ** -0.5),
        "mix_norm": gain((DEPTH, D_MODEL)),
        "w_in": nrm((DEPTH, D_MODEL, D_IN), D_MODEL ** -0.5),
        "lru_conv_w": nrm((DEPTH, CONV_W, D_LRU), CONV_W ** -0.5),
        "lru_conv_b": nrm((DEPTH, D_LRU), 0.02),
        "lru_gate_a_w": nrm((DEPTH, LRU_HEADS, LRU_BS, LRU_BS), LRU_BS ** -0.5),
        "lru_gate_a_b": nrm((DEPTH, D_LRU), 0.02),
        "lru_gate_x_w": nrm((DEPTH, LRU_HEADS, LRU_BS, LRU_BS), LRU_BS ** -0.5),
        "lru_gate_x_b": nrm((DEPTH, D_LRU), 0.02),
        "lru_lambda": lru_lambda,
        "lru_out_norm": gain((DEPTH, D_LRU)),
        "ssd_conv_w": nrm((DEPTH, CONV_W, D_XBC), CONV_W ** -0.5),
        "ssd_conv_b": nrm((DEPTH, D_XBC), 0.02),
        "ssd_dt_bias": ssd_dt_bias,
        "ssd_a_log": ssd_a_log,
        "ssd_d": 1.0 + nrm((DEPTH, SSD_HEADS), 0.1),
        "ssd_norm": gain((DEPTH, D_SSD)),
        "w_out": nrm((DEPTH, D_MIX, D_MODEL), D_MIX ** -0.5),
        "ffn2_norm": gain((DEPTH, D_MODEL)),
        "ffn2_w_gate": nrm((DEPTH, D_MODEL, D_FF), D_MODEL ** -0.5),
        "ffn2_w_up": nrm((DEPTH, D_MODEL, D_FF), D_MODEL ** -0.5),
        "ffn2_w_down": nrm((DEPTH, D_FF, D_MODEL), D_FF ** -0.5),
        "final_norm": gain((D_MODEL,)),
    }

def reference(x_prompt, x_sample, state_lru_conv, state_lru_h, state_ssd_conv, state_ssd_h,
              ffn1_norm, ffn1_w_gate, ffn1_w_up, ffn1_w_down, mix_norm, w_in,
              lru_conv_w, lru_conv_b, lru_gate_a_w, lru_gate_a_b, lru_gate_x_w, lru_gate_x_b,
              lru_lambda, lru_out_norm, ssd_conv_w, ssd_conv_b, ssd_dt_bias, ssd_a_log, ssd_d,
              ssd_norm, w_out, ffn2_norm, ffn2_w_gate, ffn2_w_up, ffn2_w_down, final_norm):
    xp = x_prompt
    xs = x_sample
    p_states = []
    s_states = []
    for l in range(DEPTH):
        lw = (ffn1_norm[l], ffn1_w_gate[l], ffn1_w_up[l], ffn1_w_down[l], mix_norm[l], w_in[l],
              lru_conv_w[l], lru_conv_b[l], lru_gate_a_w[l], lru_gate_a_b[l], lru_gate_x_w[l],
              lru_gate_x_b[l], lru_lambda[l], lru_out_norm[l], ssd_conv_w[l], ssd_conv_b[l],
              ssd_dt_bias[l], ssd_a_log[l], ssd_d[l], ssd_norm[l], w_out[l],
              ffn2_norm[l], ffn2_w_gate[l], ffn2_w_up[l], ffn2_w_down[l])
        xp, sp = run_layer(xp,
                           jnp.zeros((BATCH, CONV_W - 1, D_LRU), xp.dtype),
                           jnp.zeros((BATCH, D_LRU), jnp.float32),
                           jnp.zeros((BATCH, CONV_W - 1, D_XBC), xp.dtype),
                           jnp.zeros((BATCH, SSD_HEADS, SSD_HEAD_DIM, SSD_STATE), jnp.float32),
                           *lw)
        xs, ss = run_layer(xs, state_lru_conv[l], state_lru_h[l], state_ssd_conv[l], state_ssd_h[l], *lw)
        p_states.append(sp)
        s_states.append(ss)
    y_prompt = rmsnorm(xp, final_norm)
    y_sample = rmsnorm(xs, final_norm)
    prompt_lru_conv = jnp.stack([s[0] for s in p_states])
    prompt_lru_h = jnp.stack([s[1] for s in p_states])
    prompt_ssd_conv = jnp.stack([s[2] for s in p_states])
    prompt_ssd_h = jnp.stack([s[3] for s in p_states])
    sample_lru_conv = jnp.stack([s[0] for s in s_states])
    sample_lru_h = jnp.stack([s[1] for s in s_states])
    sample_ssd_conv = jnp.stack([s[2] for s in s_states])
    sample_ssd_h = jnp.stack([s[3] for s in s_states])
    return (y_prompt, y_sample, prompt_lru_conv, prompt_lru_h, prompt_ssd_conv, prompt_ssd_h,
            sample_lru_conv, sample_lru_h, sample_ssd_conv, sample_ssd_h)


_drawn_inputs = setup_inputs


def setup_inputs(seed=0):
    import zlib

    import numpy as np

    out = dict(_drawn_inputs(seed))
    spreads = {}
    factors = {'lru_gate_a_b': 8.0, 'lru_gate_x_b': 8.0, 'ffn2_norm': 4.284}
    for name, (base, spread) in spreads.items():
        noise = np.random.default_rng([zlib.crc32(name.encode()), seed]).standard_normal(out[name].shape)
        drawn = base * np.exp(spread * noise) if base else spread * noise
        out[name] = __import__('jax').numpy.asarray(drawn.astype(out[name].dtype))
    for name, factor in factors.items():
        out[name] = (out[name] * factor).astype(out[name].dtype)
    return out
```

```python
from contextlib import ExitStack

import concourse.bass as bass
from concourse import mybir

F32 = mybir.dt.float32
F32R = mybir.dt.float32r
ALU = mybir.AluOpType
ACT = mybir.ActivationFunctionType
AX_X = mybir.AxisListType.X

P = 128
PROMPT, DEC = 1024, 8
T = PROMPT + DEC
CHUNKS = 3
CH = T // CHUNKS
DM, DFF = 1024, 2816
KT = DM // P
FT = DFF // P
HEADS, HD, GROUPS, NST = 16, 64, 2, 128
GH = HEADS // GROUPS
QC = 128
NCH = PROMPT // QC
XT = 12
TAPS = 4
HIST = TAPS - 1
EPS = 1e-6
LRU_C = 8.0
FFN_BLOCKS = [(0, 8), (8, 8), (16, 6)]
V_FFN1, V_MIX, V_FFN2, V_FINAL, V_LRU, V_SSD, V_D = (KT * n for n in range(7))
V_COLS = 7 * KT
PAR_TAP, PAR_BIAS, PAR_GA, PAR_GX, PAR_LAM, PAR_NEG = 0, 4, 5, 6, 7, 8
PARS = 9
CT = XT + KT


class Units:

    def __init__(self):
        self.n = 0

    def pair(self, i, s):
        return i * 2 + (self.n + s)

    def pair_of_set(self, i):
        return i + self.n // 2


def first_then_loop(eng, n, body):
    body(0)
    if n > 1:
        with eng.Fori(1, n) as i:
            body(i)


def loop(eng, n, body):
    if n == 1:
        body(0)
    else:
        with eng.Fori(0, n) as i:
            body(i)


class Weights:

    def __init__(self, nc, ctx, o, tag):
        def sem(name):
            return o.semaphore(nc, f"{tag}_{name}")

        self.nc = nc
        self.raw = [ctx.enter_context(nc.sbuf_tensor(f"{tag}_w_raw{s}", [P, KT * P], F32)) for s in range(2)]
        self.hi = [ctx.enter_context(nc.sbuf_tensor(f"{tag}_w_hi{s}", [P, KT * P], F32R)) for s in range(2)]
        self.lo = [ctx.enter_context(nc.sbuf_tensor(f"{tag}_w_lo{s}", [P, KT * P], F32R)) for s in range(2)]
        self.landed = [sem(f"weights_landed{s}") for s in range(2)]
        self.split = sem("weights_split")
        self.used = sem("unit_products_done")
        self.turn, self.load_turn = sem("split_turn"), sem("load_turn")

    def load(self, sp, units, i, s, src, nk):
        u = units.pair(i, s)
        if not (isinstance(u, int) and u < 2):
            sp.wait_ge(self.split, u - 1)
            sp.sem_inc(self.load_turn, 1)
        sp.dma_start(self.raw[s][:, 0:nk * P], src).then_inc(self.landed[s], 16)

    def split_unit(self, pool, units, i, s, nk):
        u = units.pair(i, s)
        if not (isinstance(u, int) and u < 2):
            pool.wait_ge(self.used, u - 1)
            pool.sem_inc(self.turn, 1)
        pool.wait_ge(self.landed[s], units.pair_of_set(i) * 16 + 16)
        pool.sem_inc(self.turn, 1)
        n = nk * P
        pool.tensor_scalar(self.hi[s][:, 0:n], self.raw[s][:, 0:n], 1.0, 0.0, ALU.mult, ALU.add)
        pool.drain()
        pool.tensor_tensor(self.lo[s][:, 0:n], self.raw[s][:, 0:n], self.hi[s][:, 0:n].bitcast(F32),
                           ALU.subtract).then_inc(self.split, 1)

    def products(self, pe, units, i, s, bank_set, x_hi, x_lo, nk, hooks=None, ready=None):
        u = units.pair(i, s)
        pe.wait_ge(self.split, u + 1)
        for k in range(nk):
            if hooks and k in hooks:
                hooks[k]()
            if ready:
                ready(k)
            w_hi, w_lo = (w[s][:, k * P:(k + 1) * P] for w in (self.hi, self.lo))
            for n, (w, x) in enumerate(((w_hi, x_hi), (w_hi, x_lo), (w_lo, x_hi))):
                for c in range(CHUNKS):
                    last = pe.matmul(bank_set[:, c, 0:CH], w, x[:, k, c * CH:(c + 1) * CH],
                                     start=(k == 0 and n == 0), stop=(k == nk - 1 and n == 2))
        last.then_inc(self.used, 1)


def whole(bank_set):
    return bank_set[:, 0:CHUNKS, 0:CH]


def cut(x):
    return x.rearrange("p (c t) -> p c t", c=CHUNKS)


class Norm:

    def __init__(self, nc, sem, tag, x, tmp, total, scale, ones, vecs, bank_set, eps):
        self.x, self.tmp, self.total, self.scale = x, tmp, total, scale
        self.ones, self.vecs, self.bank_set, self.eps = ones, vecs, bank_set, eps
        self.squared = sem(f"{tag}_squared")
        self.added = sem(f"{tag}_square_added")
        self.summed = sem(f"{tag}_squares_summed")
        self.rooted = sem(f"{tag}_root_taken")
        self.scaled, self.high = sem(f"{tag}_scaled"), sem(f"{tag}_high_part")
        self.done = sem(f"{tag}_normed")
        self.stored = [sem(f"{tag}_stored{n}") for n in range(2)]

    def scalar(self, act, hi=None):
        for k in range(KT):
            if k >= 2:
                act.wait_ge(self.added, k - 1)
            act.activation(self.tmp[k % 2][:], self.x[:, k, :], ACT.Square).then_inc(self.squared, 1)
        act.wait_ge(self.summed, 1)
        act.activation(cut(self.scale[:]), whole(self.bank_set), ACT.Sqrt, bias=self.eps[:, 0:1],
                       scale=1.0 / DM).then_inc(self.rooted, 1)
        if hi is not None:
            high_parts(act, self.tmp, hi, self.scaled, self.high)

    def tensor(self, pe):
        pe.wait_ge(self.added, KT)
        for c in range(CHUNKS):
            last = pe.matmul(self.bank_set[:, c, 0:CH], self.ones[:], self.total[:, c * CH:(c + 1) * CH],
                             start=True, stop=True)
        last.then_inc(self.summed, 1)

    def vector(self, dve, gain, hi=None, lo=None):
        for k in range(KT):
            dve.wait_ge(self.squared, k + 1)
            if k == 0:
                dve.tensor_copy(self.total[:], self.tmp[0][:]).then_inc(self.added, 1)
            else:
                dve.drain()
                dve.tensor_tensor(self.total[:], self.total[:], self.tmp[k % 2][:], ALU.add).then_inc(self.added, 1)
        dve.wait_ge(self.rooted, 1)
        dve.reciprocal(self.scale[:], self.scale[:])
        for k in range(KT):
            dve.drain()
            if hi is None and k >= 2:
                dve.wait_ge(self.stored[k % 2], 16 * (k // 2))
            dve.scalar_tensor_tensor(self.tmp[k % 2][:], self.x[:, k, :], self.vecs[:, gain + k:gain + k + 1],
                                     self.scale[:], ALU.mult, ALU.mult).then_inc(self.done if hi is None else self.scaled, 1)
            if hi is not None and k:
                low_part(dve, self.tmp, hi, lo, k - 1, self.high, self.done)
        if hi is not None:
            low_part(dve, self.tmp, hi, lo, KT - 1, self.high, self.done)


def high_parts(act, tmp, hi, scaled, high):
    for k in range(KT):
        act.wait_ge(scaled, k + 1)
        act.activation(hi[:, k, :], tmp[k % 2][:], ACT.Copy).then_inc(high, 1)


def low_part(dve, tmp, hi, lo, k, high, done):
    dve.drain()
    dve.wait_ge(high, k + 1)
    dve.tensor_tensor(lo[:, k, :], tmp[k % 2][:], hi[:, k, :].bitcast(F32), ALU.subtract).then_inc(done, 1)


def split_rows(dve, x, hi, lo):
    dve.tensor_copy(hi, x[:])
    dve.drain()
    return dve.tensor_tensor(lo, x[:], hi.bitcast(F32), ALU.subtract)


class Ffn:

    def __init__(self, sem, tag, weights, x, xn, h, tmp, sets):
        self.w, self.x, self.xn, self.h, self.tmp, self.sets = weights, x, xn, h, tmp, sets
        self.set_read = [sem(f"{tag}_bank_set_read{s}") for s in range(2)]
        self.hidden = sem(f"{tag}_hidden_split")
        self.hidden_made = 0

    def sync(self, sp, units, gate_up, down):
        for first, n in FFN_BLOCKS:
            def load_gate_up(i):
                for s in range(2):
                    self.w.load(sp, units, i, s, gate_up[(i + first) * 2 + s], KT)
            first_then_loop(sp, n, load_gate_up)
            units.n += 2 * n

            def load_down(i):
                for s in range(2):
                    self.w.load(sp, units, i, s, down[i * 2 + s, :, first * P:(first + n) * P], n)
            loop(sp, KT // 2, load_down)
            units.n += KT

    def pool(self, pool, units):
        for first, n in FFN_BLOCKS:
            for pairs, nk in ((n, KT), (KT // 2, n)):
                def split_pair(i):
                    for s in range(2):
                        self.w.split_unit(pool, units, i, s, nk)
                first_then_loop(pool, pairs, split_pair)
                units.n += 2 * pairs

    def wait_set(self, pe, units, i, s):
        v = units.pair_of_set(i)
        if not (isinstance(v, int) and v == 0):
            pe.wait_ge(self.set_read[s], v)

    def tensor(self, pe, units, normed):
        (x_hi, x_lo), (h_hi, h_lo) = self.xn, self.h
        hidden = 0
        for b, (first, n) in enumerate(FFN_BLOCKS):
            def gate_up(i):
                for s in range(2):
                    self.wait_set(pe, units, i, s)
                    ready = None
                    if b == 0 and isinstance(i, int) and s == 0:
                        def ready(k):
                            pe.wait_ge(normed, k + 1)
                    self.w.products(pe, units, i, s, self.sets[s], x_hi, x_lo, KT, ready=ready)
            first_then_loop(pe, n, gate_up)
            units.n += 2 * n
            hidden += n
            pe.wait_ge(self.hidden, hidden)

            def down(i):
                for s in range(2):
                    self.wait_set(pe, units, i, s)
                    self.w.products(pe, units, i, s, self.sets[s], h_hi, h_lo, n)
            loop(pe, KT // 2, down)
            units.n += KT

    def scalar(self, act, units):
        for first, n in FFN_BLOCKS:
            def gate(i):
                v = units.pair_of_set(i)
                act.wait_ge(self.w.used, units.pair(i, 0) + 1)
                if not (isinstance(v, int) and v == 0):
                    act.wait_ge(self.set_read[1], v)
                act.activation(cut(self.tmp[0][:]), whole(self.sets[0]), ACT.Silu).then_inc(self.set_read[0], 1)
            first_then_loop(act, n, gate)
            units.n += 2 * n + KT

    def vector(self, dve, units):
        (h_hi, h_lo) = self.h
        for first, n in FFN_BLOCKS:
            def hidden(i):
                dve.drain()
                dve.wait_ge(self.set_read[0], units.pair_of_set(i) + 1)
                dve.wait_ge(self.w.used, units.pair(i, 1) + 1)
                dve.tensor_tensor(cut(self.tmp[1][:]), cut(self.tmp[0][:]), whole(self.sets[1]),
                                  ALU.mult).then_inc(self.set_read[1], 1)
                dve.drain()
                split_rows(dve, self.tmp[1], h_hi[:, i, :], h_lo[:, i, :]).then_inc(self.hidden, 1)
            first_then_loop(dve, n, hidden)
            units.n += 2 * n
            self.residual(dve, units, 0.5)

    def residual(self, dve, units, factor, between=None):
        def add(i):
            for s in range(2):
                dve.drain()
                dve.wait_ge(self.w.used, units.pair(i, s) + 1)
                tile = cut(self.x[:, i * 2 + s, :])
                dve.scalar_tensor_tensor(tile, whole(self.sets[s]), factor, tile,
                                         ALU.mult, ALU.add).then_inc(self.set_read[s], 1)
                if between:
                    between(i, s)
        loop(dve, KT // 2, add)
        units.n += KT


def first_half_step(nc, o, xt, gate_up, down, x_kept):
    with ExitStack() as ctx:
        def sem(name):
            return o.semaphore(nc, name)

        x = ctx.enter_context(nc.sbuf_tensor("x1", [P, KT, T], F32))
        h = [ctx.enter_context(nc.sbuf_tensor(f"h1_{n}", [P, KT, T], F32R)) for n in ("hi", "lo")]
        sets = [ctx.enter_context(nc.psum_tensor(f"set1_{s}", [P, CHUNKS, 512], F32)) for s in range(2)]
        weights = Weights(nc, ctx, o, "a")
        norm1 = Norm(nc, sem, "ffn1", x, o.tmp, o.tmp[2], o.tmp[3], o.ones, o.vecs, sets[0], o.eps)
        norm2 = Norm(nc, sem, "mix", x, o.tmp, o.tmp[2], o.tmp[3], o.ones, o.vecs, sets[0], o.eps)
        ffn = Ffn(sem, "ffn1", weights, x, o.xn, h, o.tmp, sets)
        vecs_landed, x_landed, x_stored, consts = (sem(n) for n in ("vecs_landed", "x_landed", "x_stored", "consts_set"))
        x_tiles = [sem(f"x_tile_landed{k}") for k in range(KT)]
        downs = KT // 2 * len(FFN_BLOCKS)
        reads = sum(n for _, n in FFN_BLOCKS) + downs

        with nc.Block() as block:
            @block.sync
            def _(sp):
                sp.dma_start(o.vecs[:], o.vecs_dram).then_inc(vecs_landed, 16)
                for k in range(KT):
                    sp.dma_start(x[:, k, :], xt[:, k, :]).then_inc(x_tiles[k], 16)
                ffn.sync(sp, Units(), gate_up, down)
                for s in range(2):
                    sp.wait_ge(ffn.set_read[s], reads)
                sp.dma_start(x_kept, x[:]).then_inc(x_stored, 16)
                sp.wait_ge(x_stored, 16)

            @block.gpsimd
            def _(pool):
                pool.memset(o.ones[:], 1.0)
                pool.memset(o.eps[:], EPS).then_inc(consts, 1)
                ffn.pool(pool, Units())

            @block.scalar
            def _(act):
                act.wait_ge(consts, 1)
                for k in range(KT):
                    act.wait_ge(x_tiles[k], 16)
                norm1.scalar(act, o.xn[0])
                ffn.scalar(act, Units())
                for s in range(2):
                    act.wait_ge(ffn.set_read[s], reads)
                norm2.scalar(act, o.xn[0])

            @block.tensor
            def _(pe):
                pe.wait_ge(consts, 1)
                norm1.tensor(pe)
                pe.wait_ge(norm1.rooted, 1)
                ffn.tensor(pe, Units(), norm1.done)
                norm2.tensor(pe)

            @block.vector
            def _(dve):
                dve.wait_ge(vecs_landed, 16)
                norm1.vector(dve, V_FFN1, *o.xn)
                ffn.vector(dve, Units())
                norm2.vector(dve, V_MIX, *o.xn)



def softplus(dve, act, v, t, magnitude, exponent):
    if act is not None:
        act.wait_ge(magnitude, 1)
        act.activation(t[0], t[0], ACT.Exp, scale=-1.0).then_inc(exponent, 1)
        return None
    dve.scalar_tensor_tensor(t[0], v, -1.0, v, ALU.mult, ALU.max).then_inc(magnitude, 1)
    dve.tensor_scalar(v, v, 0.0, None, ALU.max)
    dve.wait_ge(exponent, 1)
    dve.tensor_scalar(t[1], t[0], 2.0, None, ALU.add)
    dve.drain()
    dve.reciprocal(t[1], t[1])
    dve.drain()
    dve.tensor_tensor(t[0], t[0], t[1], ALU.mult)
    dve.drain()
    dve.tensor_tensor(t[1], t[0], t[0], ALU.mult)
    dve.drain()
    dve.tensor_scalar(t[2], t[1], 1.0 / 17, None, ALU.mult)
    for n in range(15, 1, -2):
        dve.drain()
        dve.scalar_tensor_tensor(t[2], t[2], 1.0 / n, t[1], ALU.add, ALU.mult)
    dve.drain()
    dve.scalar_tensor_tensor(t[2], t[2], 1.0, t[0], ALU.add, ALU.mult)
    dve.drain()
    return dve.scalar_tensor_tensor(v, t[2], 2.0, v, ALU.mult, ALU.add)


A_BC, A_SEL, A_SEL2, A_HIST = 0, 4096, 6144, 7168
A_STATE, A_UPD = (4096, 5120), 6144
A_SLAB, A_XDD, A_E2, A_Y, A_HT, A_BTOK, A_CB = 0, 1536, 2048, 2560, 3072, 4096, 4352
A_SEL_CH, A_MASK, A_DL, A_CDEC = 4608, 6656, 6784, 6792
A_DECAY, A_GATE_A, A_GATE_X, A_SQ, A_H, A_GELU, A_SILU = (T * n for n in range(7))
A_GATES = 7 * T
ARENA = A_GATES + 4 * P


def mixer(nc, o, d):
    with ExitStack() as ctx:
        def sb(name, shape, dt=F32):
            return ctx.enter_context(nc.sbuf_tensor(name, shape, dt))

        def sem(name):
            return o.semaphore(nc, name)

        w = Weights(nc, ctx, o, "m")
        xbc = sb("xbc", [P, XT, T])
        raw = sb("conv_in", [P, HIST + T])
        accs = [sb(f"conv_out{s}", [P, T]) for s in range(2)]
        acc = accs[0]
        pars = sb("pars", [P, CT, PARS])
        par2 = [sb(f"par{s}", [P, PARS]) for s in range(2)]
        hist_sum = sb("hist_sum", [P, CT, DEC])
        tail = sb("tail", [P, CT, HIST + DEC])
        small = sb("small", [P, CT, DEC])
        heads = sb("heads", [HEADS, 2])
        dt_w = sb("dt_w", [P, KT * HEADS])
        dt_w_hi, dt_w_lo = sb("dt_w_hi", [P, KT * HEADS], F32R), sb("dt_w_lo", [P, KT * HEADS], F32R)
        ident = sb("ident", [P, P])
        token = sb("token", [P, 2, NCH, HEADS])
        dec_dt, dec_a = sb("dec_dt", [P, KT, DEC]), sb("dec_a", [P, KT, DEC])
        lru_h0, lru_h = sb("lru_h0", [P, KT, DEC]), sb("lru_h", [P, KT, 1 + DEC])
        lam = sb("lam", [P, 4, KT])
        arena = sb("arena", [P, ARENA])
        set0 = ctx.enter_context(nc.psum_tensor("mset0", [P, CHUNKS, 512], F32))
        set1 = ctx.enter_context(nc.psum_tensor("mset1", [P, CHUNKS, 512], F32))
        bank6 = ctx.enter_context(nc.psum_tensor("bank6", [P, 512], F32))
        bank7 = ctx.enter_context(nc.psum_tensor("bank7", [P, 512], F32))
        sets = (set0, set1)
        tmp = o.tmp

        def part(at, *shape):
            n = 1
            for m in shape:
                n *= m
            v = arena[:, at:at + n]
            if len(shape) == 2:
                return v.rearrange("p (a b) -> p a b", a=shape[0])
            if len(shape) == 3:
                return v.rearrange("p (a b c) -> p a b c", a=shape[0], b=shape[1])
            return v

        bc_dec = part(A_BC, DEC, 4, P)
        sel = part(A_SEL, HEADS, P)[0:HEADS]
        sel2 = part(A_SEL2, KT, 2, HD)[0:HEADS]
        hist = part(A_HIST, CT, HIST * DEC)
        state = [part(a, DEC, P) for a in A_STATE]
        upd = part(A_UPD, DEC, P)
        slab = part(A_SLAB, XT, QC)
        xdd = part(A_XDD, GH, HD)
        e2 = part(A_E2, GH // 2, QC)
        ybuf = part(A_Y, GH // 2, QC)
        ht = part(A_HT, HEADS, HD)
        btok = part(A_BTOK, GROUPS, P)
        cb = part(A_CB, GROUPS, QC)
        selc = part(A_SEL_CH, HEADS, P)[0:HEADS]
        mask = part(A_MASK, QC)
        dl, cdec = part(A_DL, GH), part(A_CDEC, GH)
        xdt = acc[:, 0:HEADS * HD].rearrange("p (h c) -> p h c", h=HEADS)
        dxs = raw[:, 0:KT * QC].rearrange("p (t c) -> p t c", t=KT)
        lmat = tmp[2][:, 0:GH * QC].rearrange("p (h c) -> p h c", h=GH)
        decay, gate_a, gate_x, sq, hbuf, gelu, silu = (
            part(a, T) for a in (A_DECAY, A_GATE_A, A_GATE_X, A_SQ, A_H, A_GELU, A_SILU))
        gates = part(A_GATES, 2, 2, P)
        dt_row, cum_row = tmp[3][0:HEADS], tmp[4][0:HEADS]
        low = [tmp[n][0:HEADS] for n in range(3)]
        bcast = set1[:, 0:2, :].rearrange("p b (h t) -> p (b h) t", t=QC)
        turned = set1[:, 0:2, :].rearrange("p b (h c) -> p (b h) c", c=HD)
        b5 = set1[:, 2, :]
        off_v = bank7[:, :].rearrange("p (t c) -> p t c", t=GH // 2)
        diag_v = bank6[:, :].rearrange("p (t c) -> p t c", t=GH // 2)

        pars_landed, hist_landed, heads_landed, dt_w_landed = (
            sem(n) for n in ("pars_landed", "hist_landed", "heads_landed", "dt_w_landed"))
        state_landed, state_stored = [sem(f"state_landed{s}") for s in range(2)], [sem(f"state_stored{s}") for s in range(2)]
        gates_landed, mates_landed, mixed_stored = sem("gates_landed"), sem("mates_landed"), sem("mixed_stored")
        outputs_stored, scratch_stored, h0_landed = sem("outputs_stored"), [sem(f"scratch_stored{n}") for n in range(2)], sem("h0_landed")
        consts, ident_ready, chunk_consts = sem("consts"), sem("ident_ready"), sem("chunk_consts")
        cleared = sem("cleared")
        lam_abs, lam_exp, dt_abs, dt_exp = sem("lam_abs"), sem("lam_exp"), sem("dt_abs"), sem("dt_exp")
        lam_done, a_exp, dt_split, dt_products, dt_read, dt_done = (
            sem(n) for n in ("lam_done", "a_exp", "dt_split", "dt_products", "dt_read", "dt_done"))
        token_major, token_read, widened, bc_turned, bc_copied, bc_wide, bc_read, bc_done = (
            sem(n) for n in ("token_major", "token_read", "widened", "bc_turned", "bc_copied",
                             "bc_wide", "bc_read", "bc_done"))
        dec_exp = sem("dec_exp")
        set_read = [sem(f"m_bank_set_read{s}") for s in range(2)]
        convolved, xbc_ready = sem("convolved"), sem("xbc_ready")
        state_new, dec_y = sem("state_new"), sem("dec_y")
        slab_ready, x_turned, xdt_ready, cb_products = (
            sem(n) for n in ("slab_ready", "x_turned", "xdt_ready", "cb_products"))
        rows_wide, rows_read, seg_ready, exp_ready, lmat_ready, y_products, state_products = (
            sem(n) for n in ("rows_wide", "rows_read", "seg_ready", "exp_ready", "lmat_ready", "y_products", "state_products"))
        y_done, state_done, dxs_ready, proj_read = (
            sem(n) for n in ("y_done", "state_done", "dxs_ready", "proj_read"))
        pool_turn, widen_turn = sem("pool_turn"), sem("widen_turn")
        lru_read = [sem(f"lru_bank_set_read{s}") for s in range(2)]
        gate_products, gate_read, decays_ready, power_ready, root_ready = (
            sem(n) for n in ("gate_products", "gate_read", "decays_ready", "power_ready", "root_ready"))
        mixed_ready, gated_ready, squared, square_added = (
            sem(n) for n in ("mixed_ready", "gated_ready", "mixed_squared", "mixed_square_added"))
        sums, roots, scales = sem("norm_sums"), sem("norm_roots"), sem("norm_scales")

        A1, A2, PA, PB = 2, 4, 8, 4
        STATE_COLS = DEC * NST

        with nc.Block() as block:
            @block.sync
            def _(sp):
                sp.dma_start(dt_w[:], d.w_dt).then_inc(dt_w_landed, 16)
                sp.dma_start(pars[:], d.pars).then_inc(pars_landed, 16)
                sp.dma_start(hist, d.hist).then_inc(hist_landed, 16)
                sp.dma_start(heads[:], d.heads).then_inc(heads_landed, 16)
                sp.dma_start(lru_h0[:], d.lru_h0).then_inc(h0_landed, 16)
                sp.dma_start(d.kept_out, d.hist[:, :, DEC:]).then_inc(outputs_stored, 16)
                units = Units()

                def load_pair(i):
                    for s in range(2):
                        w.load(sp, units, i, s, d.w_in[i * 2 + units.n + s], KT)

                first_then_loop(sp, A1, load_pair)
                units.n += 2 * A1

                def load_x(i):
                    for s in range(2):
                        w.load(sp, units, i, s, d.w_in[i * 2 + units.n + s], KT)
                        if isinstance(i, int):
                            sp.wait_ge(bc_done, 1)
                        else:
                            sp.wait_ge(state_stored[s], i * 16)
                            sp.sem_inc(w.load_turn, 1)
                            sp.wait_ge(dec_y, i * 2 + (s - 1))
                            sp.sem_inc(w.load_turn, 1)
                        sp.dma_start(state[s], d.state_in[i * 2 + s]).then_inc(state_landed[s], 16)
                first_then_loop(sp, A2, load_x)
                units.n += 2 * A2
                loop(sp, PA, load_pair)
                units.n += 2 * PA
                loop(sp, PB, load_pair)
                sp.wait_ge(mixed_ready, KT)
                sp.dma_start(d.tail_out, tail[:]).then_inc(outputs_stored, 16)
                sp.dma_start(d.lru_h_out, lru_h[:]).then_inc(outputs_stored, 16)
                sp.wait_ge(outputs_stored, 64)

            @block.gpsimd
            def _(pool):
                units = Units()
                pool.memset(ident[:], 0.0)
                pool.memset(arena[:, A_SEL:A_SEL + HEADS * P], 0.0)
                pool.memset(arena[:, A_SEL2:A_SEL2 + HEADS * HD], 0.0).then_inc(cleared, 1)
                pool.wait_ge(cleared, 1)
                pool.affine_select(out=ident[:], in_=ident[:], compare_op=ALU.not_equal, fill=1.0, base=0,
                                   pattern=[[-1, P]], channel_multiplier=1)
                pool.affine_select(out=sel, in_=sel, compare_op=ALU.not_equal, fill=1.0, base=0,
                                   pattern=[[-1, HEADS], [0, P]], channel_multiplier=1)
                pool.affine_select(out=sel2, in_=sel2, compare_op=ALU.not_equal, fill=1.0, base=0,
                                   pattern=[[-2, KT], [-1, 2], [0, HD]], channel_multiplier=1)
                pool.memset(raw[:, 0:HIST], 0.0).then_inc(ident_ready, 1)

                def split_pair(i):
                    for s in range(2):
                        w.split_unit(pool, units, i, s, KT)

                first_then_loop(pool, A1 + A2, split_pair)
                units.n += 2 * (A1 + A2)
                pool.wait_ge(dec_y, KT)
                for s in range(2):
                    pool.wait_ge(state_stored[s], 16 * (KT // 2))
                pool.memset(arena[:, A_SEL_CH:A_SEL_CH + HEADS * P], 0.0)
                pool.memset(ht, 0.0)
                pool.memset(mask, 1.0).then_inc(cleared, 1)
                pool.wait_ge(cleared, 2)
                pool.affine_select(out=selc, in_=selc, compare_op=ALU.not_equal, fill=1.0, base=0,
                                   pattern=[[-1, HEADS], [0, P]], channel_multiplier=1)
                pool.affine_select(out=mask, in_=mask, compare_op=ALU.is_ge, fill=0.0, base=0,
                                   pattern=[[1, QC]], channel_multiplier=-1).then_inc(chunk_consts, 1)

                def chunk(c):
                    for s in range(2):
                        w.split_unit(pool, units, c, s, KT)
                    pool.wait_ge(slab_ready, c + 1)
                    pool.sem_inc(pool_turn, 1)
                    if not isinstance(c, int):
                        pool.wait_ge(y_done, c * 2)
                        pool.sem_inc(pool_turn, 1)
                    gain = o.vecs[:, V_D:V_D + KT].unsqueeze(2).broadcast_to([P, KT, QC])
                    pool.tensor_tensor(dxs, slab[:, 4:XT, :], gain, ALU.mult).then_inc(dxs_ready, 1)
                first_then_loop(pool, PA, chunk)
                units.n += 2 * PA
                pool.wait_ge(y_done, 2 * NCH)
                pool.memset(raw[:, 0:HIST], 0.0).then_inc(chunk_consts, 1)
                loop(pool, PB, split_pair)

            @block.tensor
            def _(pe):
                units = Units()
                x_hi, x_lo = o.xn
                pe.wait_ge(dt_split, 1)
                for k in range(KT):
                    w_hi, w_lo = (v[:, k * HEADS:(k + 1) * HEADS] for v in (dt_w_hi, dt_w_lo))
                    for n, (ww, x) in enumerate(((w_hi, x_hi), (w_hi, x_lo), (w_lo, x_hi))):
                        for c in range(CHUNKS):
                            last = pe.matmul(set0[0:HEADS, c, 0:CH], ww, x[:, k, c * CH:(c + 1) * CH],
                                             start=(k == 0 and n == 0), stop=(k == KT - 1 and n == 2))
                last.then_inc(dt_products, 1)
                pe.wait_ge(dt_read, 1)

                def project(i):
                    for s in range(2):
                        v = units.pair_of_set(i)
                        if not (isinstance(v, int) and v == 0):
                            pe.wait_ge(set_read[s], v)
                        w.products(pe, units, i, s, sets[s], x_hi, x_lo, KT)
                first_then_loop(pe, A1, project)
                units.n += 2 * A1

                pe.wait_ge(ident_ready, 1)
                pe.wait_ge(dt_done, 1)
                tok = bank6[:, 0:2 * NCH * HEADS].rearrange("p (a c h) -> p a c h", a=2, c=NCH)
                for n, row in enumerate((dt_row, cum_row)):
                    for c in range(NCH):
                        last = pe.transpose(tok[:, n, c, :], row[:, c * QC:(c + 1) * QC], ident[0:HEADS, 0:HEADS])
                last.then_inc(token_major, 1)
                wide = bank7[:, 0:KT * 2 * DEC].rearrange("p (t a b) -> p t a b", t=KT, a=2)
                for t in range(KT):
                    both = sel2[:, t].rearrange("k e c -> k (e c)")
                    for n, row in enumerate((dt_row, cum_row)):
                        last = pe.matmul(wide[:, t, n, :], both, row[:, PROMPT:T], start=True, stop=True)
                last.then_inc(widened, 1)
                pe.wait_ge(xbc_ready, 4)
                pe.wait_ge(token_read, 1)
                for m in range(4):
                    last = pe.transpose(bank6[0:DEC, m * P:(m + 1) * P], xbc[:, m, PROMPT:T], ident[:])
                last.then_inc(bc_turned, 1)
                pe.wait_ge(bc_copied, 1)
                pe.wait_ge(dec_exp, 1)
                for b in range(DEC):
                    if b >= 2:
                        pe.wait_ge(bc_read, b - 1)
                    pe.matmul((bank6, bank7)[b % 2][:], sel[0:DEC, b, :], tmp[0][0:DEC, 0:4 * P],
                              start=True, stop=True).then_inc(bc_wide, 1)

                loop(pe, A2, project)
                units.n += 2 * A2
                for s in range(2):
                    pe.wait_ge(set_read[s], A1 + A2)
                pe.wait_ge(chunk_consts, 1)
                pe.wait_ge(bc_done, 1)

                def chunk(c):
                    def turn_x():
                        pe.wait_ge(slab_ready, c + 1)
                        for t in range(KT):
                            last = pe.transpose(set1[:, t // 4, t % 4 * P:(t % 4 + 1) * P], slab[:, 4 + t, :], ident[:])
                        last.then_inc(x_turned, 1)

                    def turn_b():
                        for g in range(GROUPS):
                            pe.transpose(b5[:, g * P:(g + 1) * P], slab[:, g, :], ident[:])
                        for g in range(GROUPS):
                            last = pe.matmul(b5[:, (2 + g) * P:(3 + g) * P], slab[:, g, :], slab[:, 2 + g, :],
                                             start=True, stop=True)
                        last.then_inc(cb_products, 1)

                    def widen(g):
                        if g == 0:
                            pe.wait_ge(xdt_ready, c + 1)
                        else:
                            pe.wait_ge(exp_ready, c * 2 + 1)
                        pe.sem_inc(widen_turn, 1)
                        for h in range(GH):
                            last = pe.matmul(set1[:, h // 4, h % 4 * QC:(h % 4 + 1) * QC], selc[:, g * GH + h, :],
                                             cum_row[:, bass.ds(c * QC, QC)], start=True, stop=True)
                        last.then_inc(rows_wide, 1)

                    def outputs(g):
                        pe.wait_ge(lmat_ready, c * 2 + (g + 1))
                        if not isinstance(c, int) or g:
                            pe.wait_ge(y_done, c * 2 + g)
                            pe.wait_ge(state_done, c * 2 + g)
                        for h in range(GH):
                            pe.matmul(bank6[h % 2 * HD:(h % 2 + 1) * HD, h // 2 * QC:(h // 2 + 1) * QC],
                                      xdt[:, g * GH + h, :], lmat[:, h, :], start=True, stop=True)
                        for t in range(GH // 2):
                            last = pe.matmul(bank7[:, t * QC:(t + 1) * QC],
                                             ht[:, g * GH + 2 * t:g * GH + 2 * t + 2, :].rearrange("p h c -> p (h c)"),
                                             slab[:, 2 + g, :], start=True, stop=True)
                        last.then_inc(y_products, 1)
                        pe.matmul(b5, btok[:, g, :], xdd.rearrange("p h c -> p (h c)"),
                                  start=True, stop=True).then_inc(state_products, 1)

                    if not isinstance(c, int):
                        pe.wait_ge(proj_read, c * 2)
                        pe.wait_ge(state_done, c * 2)
                    turn_x()
                    w.products(pe, units, c, 0, set0, x_hi, x_lo, KT,
                               hooks={2: turn_b, 5: lambda: widen(0)})
                    pe.wait_ge(proj_read, c * 2 + 1)
                    w.products(pe, units, c, 1, set0, x_hi, x_lo, KT,
                               hooks={3: lambda: (outputs(0), widen(1))})
                    outputs(1)
                first_then_loop(pe, NCH, chunk)
                units.n += 2 * PA
                pe.wait_ge(proj_read, 2 * PA)
                pe.wait_ge(y_done, 2 * NCH)
                pe.wait_ge(state_done, 2 * NCH)

                def gate(i, s):
                    pe.wait_ge(convolved, i * 2 + (XT + s + 1))
                    pe.wait_ge(gates_landed, i * 16 + 16)
                    for c in range(CHUNKS):
                        v = i * (2 * CHUNKS) + (s * CHUNKS + c)
                        if not (isinstance(v, int) and v == 0):
                            pe.wait_ge(gate_read, v)
                        for n, bank in enumerate((bank6, bank7)):
                            last = pe.matmul(bank[:, 0:CH], gates[:, s, n, :], accs[s][:, c * CH:(c + 1) * CH],
                                             start=True, stop=True)
                        last.then_inc(gate_products, 1)

                def lru_pair(i):
                    for s in range(2):
                        if not isinstance(i, int):
                            pe.wait_ge(lru_read[s], i)
                        w.products(pe, units, i, s, sets[s], x_hi, x_lo, KT)
                        if s == 1:
                            gate(i, 0)
                        elif not isinstance(i, int):
                            gate(i - 1, 1)
                first_then_loop(pe, PB, lru_pair)
                gate(PB - 1, 1)
                for n in range(3):
                    if n == 0:
                        pe.wait_ge(square_added, KT)
                        pe.wait_ge(lru_read[0], PB)
                    else:
                        pe.wait_ge(roots, n)
                    for c in range(CHUNKS):
                        last = pe.matmul(set0[:, c, 0:CH], o.ones[:], tmp[2 + n][:, c * CH:(c + 1) * CH],
                                         start=True, stop=True)
                    last.then_inc(sums, 1)

            def copy_raw(act, units, i, s, q, read):
                act.wait_ge(w.used, units.pair(i, s) + 1)
                if not (isinstance(q, int) and q == 0):
                    act.wait_ge(convolved, q)
                act.activation(cut(raw[:, HIST:HIST + T]), whole(sets[s]), ACT.Copy).then_inc(read[s], 1)

            @block.scalar
            def _(act):
                units = Units()
                act.wait_ge(heads_landed, 16)
                act.activation(heads[:, 1:2], heads[:, 1:2], ACT.Exp).then_inc(a_exp, 1)
                softplus(None, act, None, [lam[:, 1, :]], lam_abs, lam_exp)
                softplus(None, act, None, [low[0]], dt_abs, dt_exp)
                act.wait_ge(ident_ready, 1)

                def xbc_tile(i, s):
                    q = i * 2 + (units.n + s)
                    copy_raw(act, units, i, s, q, set_read)
                    act.wait_ge(convolved, q + 1)
                    act.activation(xbc[:, q, :], acc[:], ACT.Silu).then_inc(xbc_ready, 1)

                def bc_pair(i):
                    for s in range(2):
                        xbc_tile(i, s)
                first_then_loop(act, A1, bc_pair)
                units.n += 2 * A1
                act.wait_ge(widened, 1)
                act.activation(dec_dt[:], bank7[:, 0:KT * 2 * DEC].rearrange("p (t a b) -> p t a b", t=KT, a=2)[:, :, 0, :],
                               ACT.Copy)
                act.activation(dec_a[:], bank7[:, 0:KT * 2 * DEC].rearrange("p (t a b) -> p t a b", t=KT, a=2)[:, :, 1, :],
                               ACT.Exp).then_inc(dec_exp, 1)
                act.wait_ge(bc_turned, 1)
                act.activation(tmp[0][0:DEC, 0:4 * P], bank6[0:DEC, :], ACT.Copy).then_inc(bc_copied, 1)
                for b in range(DEC):
                    act.wait_ge(bc_wide, b + 1)
                    act.activation(bc_dec[:, b], (bank6, bank7)[b % 2][:].rearrange("p (a c) -> p a c", a=4),
                                   ACT.Copy).then_inc(bc_read, 1)
                act.wait_ge(bc_read, DEC)
                act.sem_inc(bc_done, 1)

                def x_pair(i):
                    for s in range(2):
                        xbc_tile(i, s)
                        t = i * 2 + s
                        if isinstance(t, int) and t == 0:
                            continue
                        act.wait_ge(state_new, t)
                        act.dma_start(d.state_out[i * 2 + (s - 1)], state[1 - s]).then_inc(state_stored[1 - s], 16)
                first_then_loop(act, A2, x_pair)
                units.n += 2 * A2
                act.wait_ge(state_new, KT)
                act.dma_start(d.state_out[KT - 1], state[1]).then_inc(state_stored[1], 16)

                def chunk(c):
                    def exps(g):
                        act.wait_ge(rows_read, c * 2 + (g + 1))
                        if not isinstance(c, int) or g:
                            act.wait_ge(y_done, c * 2 + g)
                            act.wait_ge(state_done, c * 2 + g)
                        for e in range(2):
                            act.activation(e2[e * HD:(e + 1) * HD], bcast[e * HD:(e + 1) * HD, e::2, :], ACT.Exp)
                        act.activation(cdec, bcast[:, :, QC - 1], ACT.Exp)
                        act.wait_ge(seg_ready, c * 2 + (g + 1))
                        act.activation(lmat, lmat, ACT.Exp)
                        act.activation(dl, dl, ACT.Exp).then_inc(exp_ready, 1)

                    def keep(n, func, to):
                        act.wait_ge(w.used, units.pair(c, n) + 1)
                        if not isinstance(c, int):
                            act.wait_ge(scratch_stored[n], c * 16)
                        act.activation(cut(tmp[n][:]), whole(set0), func).then_inc(proj_read, 1)
                        act.wait_ge(proj_read, c * 2 + (n + 1))
                        act.dma_start(to[c], tmp[n][:]).then_inc(scratch_stored[n], 16)

                    exps(0)
                    keep(0, ACT.Silu, d.silu_z)
                    exps(1)
                    keep(1, ACT.Gelu_apprx_tanh, d.gelu_y)
                first_then_loop(act, NCH, chunk)
                units.n += 2 * PA
                act.wait_ge(state_done, 2 * NCH)
                act.dma_start(d.prompt_state, ht.rearrange("p h c -> p (h c)")).then_inc(outputs_stored, 16)
                act.wait_ge(outputs_stored, 32)
                for n in range(2):
                    act.wait_ge(scratch_stored[n], 16 * NCH)
                act.wait_ge(chunk_consts, 2)

                def lru_tile(i, s, last=False):
                    t = i * 2 + s
                    first = isinstance(t, int) and t == 0
                    par = par2[s]
                    if not last:
                        n, m = (i, 1) if s == 0 else (i + 1, 0)
                        copy_raw(act, units, n, m, n * 2 + (XT + m), lru_read)
                    if s == 0:
                        if not isinstance(i, int):
                            act.wait_ge(gate_products, i * (2 * CHUNKS))
                        act.dma_start(gates.rearrange("p s n c -> p (s n c)"), d.gates[i]).then_inc(gates_landed, 16)
                    if not first:
                        act.wait_ge(mixed_ready, t)
                        act.wait_ge(squared, i * 4 + 2 * s)
                        act.wait_ge(mixed_stored, i * 64 + 32 * s)
                    act.dma_start(gelu, d.gelu_y[i * 2 + s]).then_inc(mates_landed, 16)
                    act.dma_start(silu, d.silu_z[i * 2 + s]).then_inc(mates_landed, 16)
                    act.wait_ge(convolved, i * 2 + (XT + s + 1))
                    for c in range(CHUNKS):
                        act.wait_ge(gate_products, i * (2 * CHUNKS) + (s * CHUNKS + c + 1))
                        at = slice(c * CH, (c + 1) * CH)
                        act.activation(gate_a[:, at], bank6[:, 0:CH], ACT.Sigmoid, bias=par[:, PAR_GA:PAR_GA + 1])
                        act.activation(gate_x[:, at], bank7[:, 0:CH], ACT.Sigmoid,
                                       bias=par[:, PAR_GX:PAR_GX + 1]).then_inc(gate_read, 1)
                    act.drain()
                    act.activation(decay, gate_a, ACT.Exp, scale=par[:, PAR_LAM:PAR_LAM + 1])
                    act.drain()
                    act.activation(gate_a, gate_a, ACT.Tanh, scale=par[:, PAR_NEG:PAR_NEG + 1])
                    act.activation(sq, decay, ACT.Square).then_inc(decays_ready, 1)
                    act.wait_ge(power_ready, i * 2 + (s + 1))
                    act.activation(sq, sq, ACT.Sqrt).then_inc(root_ready, 1)
                    act.wait_ge(gated_ready, i * 2 + (s + 1))
                    act.dma_start(d.mixed[i * 2 + (KT + s)], silu).then_inc(mixed_stored, 16)
                    act.activation(tmp[1][:], silu, ACT.Square).then_inc(squared, 1)
                    act.wait_ge(mixed_ready, i * 2 + (s + 1))
                    act.dma_start(d.mixed[i * 2 + s], gelu).then_inc(mixed_stored, 16)
                    act.activation(tmp[0][:], gelu, ACT.Square).then_inc(squared, 1)
                copy_raw(act, units, 0, 0, XT, lru_read)
                for s in range(2):
                    lru_tile(0, s)
                with act.Fori(1, PB - 1) as i:
                    for s in range(2):
                        lru_tile(i, s)
                for s in range(2):
                    lru_tile(PB - 1, s, last=(s == 1))
                for n in range(3):
                    act.wait_ge(sums, n + 1)
                    act.activation(cut(tmp[2 + n][:]), whole(set0), ACT.Sqrt, bias=o.eps[:, 0:1],
                                   scale=(1.0 / DM if n == 0 else 2.0 / DM)).then_inc(roots, 1)
                act.wait_ge(mixed_stored, 16 * 2 * KT)

            @block.vector
            def _(dve):
                units = Units()
                dve.wait_ge(pars_landed, 16)
                dve.tensor_scalar(lam[:, 0, :], pars[:, XT:CT, PAR_LAM], -1.0, None, ALU.mult)
                dve.drain()
                softplus(dve, None, lam[:, 0, :], [lam[:, n, :] for n in (1, 2, 3)], lam_abs, lam_exp)
                dve.drain()
                dve.tensor_scalar(pars[:, XT:CT, PAR_LAM], lam[:, 0, :], -LRU_C, None, ALU.mult)
                dve.tensor_scalar(pars[:, XT:CT, PAR_NEG], lam[:, 0, :], LRU_C, None, ALU.mult)
                dve.wait_ge(hist_landed, 16)
                for k in range(HIST):
                    to = small if k else hist_sum
                    dve.tensor_tensor(to[:], hist[:, :, k * DEC:(k + 1) * DEC],
                                      pars[:, :, k:k + 1].broadcast_to([P, CT, DEC]), ALU.mult)
                    dve.drain()
                    if k:
                        dve.tensor_tensor(hist_sum[:], hist_sum[:], small[:], ALU.add)
                        dve.drain()
                dve.wait_ge(dt_w_landed, 16)
                split_rows(dve, dt_w, dt_w_hi[:], dt_w_lo[:]).then_inc(dt_split, 1)
                dve.wait_ge(heads_landed, 16)
                dve.wait_ge(dt_products, 1)
                dve.tensor_scalar(cut(dt_row), set0[0:HEADS, 0:CHUNKS, 0:CH], heads[:, 0:1], None, ALU.add).then_inc(dt_read, 1)
                dve.drain()
                softplus(dve, None, dt_row, low, dt_abs, dt_exp)
                dve.drain()
                dve.wait_ge(a_exp, 1)
                dve.tensor_scalar(cum_row, dt_row, heads[:, 1:2], -1.0, ALU.mult, ALU.mult)
                dve.memset(low[0][:, 0:PROMPT], 1.0)
                dve.drain()
                dve.memset(low[0][:, 0:PROMPT].rearrange("h (c t) -> h c t", t=QC)[:, :, 0:1], 0.0)
                dve.drain()
                dve.tensor_tensor_scan(cum_row[:, 0:PROMPT], low[0][:, 0:PROMPT], cum_row[:, 0:PROMPT], 0.0,
                                       ALU.mult, ALU.add).then_inc(dt_done, 1)

                def convolve(q, read, v, acc, par):
                    dve.wait_ge(read, v)
                    dve.tensor_copy(par[:], pars[:, q, :])
                    dve.tensor_copy(tail[:, q, :], raw[:, PROMPT:HIST + T])
                    dve.drain()
                    dve.tensor_scalar(acc[:], raw[:, HIST:HIST + T], par[:, HIST:HIST + 1], par[:, PAR_BIAS:PAR_BIAS + 1],
                                      ALU.mult, ALU.add)
                    for k in range(HIST):
                        dve.drain()
                        last = dve.scalar_tensor_tensor(acc[:, 0:PROMPT], raw[:, k:k + PROMPT], par[:, k:k + 1],
                                                        acc[:, 0:PROMPT], ALU.mult, ALU.add)
                        if k == 0:
                            dve.tensor_tensor(acc[:, PROMPT:T], acc[:, PROMPT:T], hist_sum[:, q, :], ALU.add)
                    last.then_inc(convolved, 1)

                def xbc_tile(i, s):
                    q = i * 2 + (units.n + s)
                    dve.drain()
                    if not (isinstance(q, int) and q == 0):
                        dve.wait_ge(xbc_ready, q)
                    convolve(q, set_read[s], units.pair_of_set(i) + 1, acc, par2[0])

                def bc_pair(i):
                    for s in range(2):
                        xbc_tile(i, s)
                first_then_loop(dve, A1, bc_pair)
                units.n += 2 * A1
                dve.wait_ge(token_major, 1)
                dve.tensor_copy(token[:], bank6[:, 0:2 * NCH * HEADS].rearrange("p (a c h) -> p a c h", a=2, c=NCH)).then_inc(token_read, 1)
                dve.wait_ge(dec_exp, 1)
                dve.wait_ge(bc_done, 1)

                def decode(i, s, g):
                    t = i * 2 + s
                    q = i * 2 + (4 + s)
                    xd = xbc[:, q, PROMPT:T]
                    dve.drain()
                    dve.wait_ge(xbc_ready, i * 2 + (4 + s + 1))
                    dve.tensor_tensor(small[:, 0, :], xd, dec_dt[:, t, :], ALU.mult)
                    dve.wait_ge(state_landed[s], i * 16 + 16)
                    dve.tensor_tensor(state[s], state[s], dec_a[:, t, :].unsqueeze(2).broadcast_to([P, DEC, P]), ALU.mult)
                    dve.drain()
                    dve.tensor_tensor(upd, bc_dec[:, :, g, :], small[:, 0, :].unsqueeze(2).broadcast_to([P, DEC, P]), ALU.mult)
                    dve.drain()
                    dve.tensor_tensor(state[s], state[s], upd, ALU.add).then_inc(state_new, 1)
                    dve.drain()
                    dve.tensor_tensor(upd, state[s], bc_dec[:, :, 2 + g, :], ALU.mult)
                    dve.drain()
                    dve.tensor_reduce(small[:, 1, :], upd, AX_X, ALU.add)
                    dve.drain()
                    dve.scalar_tensor_tensor(xd, xd, o.vecs[:, bass.ds(t + V_D, 1)], small[:, 1, :],
                                             ALU.mult, ALU.add).then_inc(dec_y, 1)

                for g in range(GROUPS):
                    def x_pair(j):
                        i = j + g * (A2 // 2)
                        for s in range(2):
                            xbc_tile(i, s)
                            decode(i, s, g)
                    loop(dve, A2 // 2, x_pair)
                units.n += 2 * A2

                dve.wait_ge(chunk_consts, 1)
                for s in range(2):
                    dve.wait_ge(state_stored[s], 16 * (KT // 2))

                def chunk(c):
                    at = bass.ds(c * QC, QC)
                    dve.drain()
                    if not isinstance(c, int):
                        dve.wait_ge(state_products, c * 2)
                        dve.wait_ge(dxs_ready, c)
                    dve.tensor_copy(slab, xbc[:, :, at]).then_inc(slab_ready, 1)
                    dve.wait_ge(x_turned, c + 1)
                    dve.tensor_tensor(xdt, turned, token[:, 0, c, :].unsqueeze(2).broadcast_to([P, HEADS, HD]),
                                      ALU.mult).then_inc(xdt_ready, 1)
                    dve.wait_ge(cb_products, c + 1)
                    dve.tensor_copy(btok, b5[:, 0:2 * P].rearrange("p (g n) -> p g n", g=2))
                    dve.tensor_tensor(cb, b5[:, 2 * P:4 * P].rearrange("p (g i) -> p g i", g=2),
                                      mask.unsqueeze(1).broadcast_to([P, GROUPS, QC]), ALU.mult)
                    for g in range(GROUPS):
                        heads_of = slice(g * GH, (g + 1) * GH)
                        cum = token[:, 1, c, heads_of]
                        dve.drain()
                        dve.wait_ge(rows_wide, c * 2 + (g + 1))
                        if not isinstance(c, int) or g:
                            dve.wait_ge(y_products, c * 2 + g)
                        dve.tensor_tensor(lmat, bcast, cum.unsqueeze(2).broadcast_to([P, GH, QC]), ALU.subtract)
                        dve.tensor_tensor(dl, bcast[:, :, QC - 1], cum, ALU.subtract).then_inc(rows_read, 1)
                        dve.drain()
                        dve.tensor_scalar(lmat, lmat, 0.0, None, ALU.min).then_inc(seg_ready, 1)
                        dve.wait_ge(exp_ready, c * 2 + (g + 1))
                        if not isinstance(c, int) or g:
                            dve.wait_ge(state_products, c * 2 + g)
                        dve.tensor_tensor(xdd, xdt[:, heads_of, :], dl.unsqueeze(2).broadcast_to([P, GH, HD]), ALU.mult)
                        dve.tensor_tensor(lmat, lmat, cb[:, g:g + 1, :].broadcast_to([P, GH, QC]), ALU.mult).then_inc(lmat_ready, 1)
                        dve.drain()
                        dve.wait_ge(y_products, c * 2 + (g + 1))
                        dve.tensor_tensor(ybuf, off_v, e2, ALU.mult)
                        dve.drain()
                        dve.tensor_tensor(ybuf, ybuf, diag_v, ALU.add)
                        dve.drain()
                        if g == 0:
                            dve.wait_ge(dxs_ready, c + 1)
                        dve.tensor_tensor(xbc[:, 4 + 4 * g:8 + 4 * g, at], ybuf, dxs[:, 4 * g:4 * g + 4, :],
                                          ALU.add).then_inc(y_done, 1)
                        dve.tensor_tensor(ht[:, heads_of, :], ht[:, heads_of, :],
                                          cdec.unsqueeze(2).broadcast_to([P, GH, HD]), ALU.mult)
                        dve.drain()
                        dve.wait_ge(state_products, c * 2 + (g + 1))
                        dve.tensor_tensor(ht[:, heads_of, :], ht[:, heads_of, :],
                                          b5.rearrange("p (h c) -> p h c", h=GH), ALU.add).then_inc(state_done, 1)
                first_then_loop(dve, NCH, chunk)

                dve.wait_ge(h0_landed, 16)
                dve.wait_ge(outputs_stored, 32)
                for n in range(3):
                    dve.memset(tmp[2 + n][:], 0.0)

                def lru_tile(i, s, g):
                    t = i * 2 + s
                    acc = accs[s]
                    dve.drain()
                    if t < KT - 1:
                        if t:
                            dve.wait_ge(gate_products, t * CHUNKS)
                        convolve(XT + t + 1, lru_read[1 - s], (t + 1) // 2 + 1, accs[1 - s], par2[1 - s])
                    dve.wait_ge(mates_landed, i * 64 + (32 * s + 32))
                    dve.tensor_tensor(silu, silu, xbc[:, i * 2 + (4 + s), :], ALU.mult).then_inc(gated_ready, 1)
                    dve.wait_ge(gate_read, i * (2 * CHUNKS) + (s + 1) * CHUNKS)
                    dve.tensor_tensor(gate_x, gate_x, acc[:], ALU.mult)
                    dve.wait_ge(decays_ready, i * 2 + (s + 1))
                    dve.scalar_tensor_tensor(sq, sq, 1.0, gate_a, ALU.add, ALU.mult).then_inc(power_ready, 1)
                    dve.wait_ge(squared, i * 4 + (2 * s + 1))
                    dve.tensor_tensor(tmp[3 + g][:], tmp[3 + g][:], tmp[1][:], ALU.add)
                    dve.drain()
                    dve.wait_ge(root_ready, i * 2 + (s + 1))
                    dve.tensor_tensor(gate_x, gate_x, sq, ALU.mult)
                    dve.tensor_tensor(hbuf[:, PROMPT:T], decay[:, PROMPT:T], lru_h0[:, t, :], ALU.mult)
                    dve.drain()
                    dve.tensor_tensor(hbuf[:, PROMPT:T], hbuf[:, PROMPT:T], gate_x[:, PROMPT:T], ALU.add)
                    dve.tensor_tensor_scan(hbuf[:, 0:PROMPT], decay[:, 0:PROMPT], gate_x[:, 0:PROMPT], 0.0, ALU.mult, ALU.add)
                    dve.drain()
                    dve.tensor_copy(lru_h[:, t, :], hbuf[:, PROMPT - 1:T])
                    dve.tensor_tensor(gelu, gelu, hbuf, ALU.mult).then_inc(mixed_ready, 1)
                    dve.drain()
                    dve.wait_ge(squared, i * 4 + (2 * s + 2))
                    dve.tensor_tensor(tmp[2][:], tmp[2][:], tmp[0][:], ALU.add).then_inc(square_added, 1)

                dve.drain()
                convolve(XT, lru_read[0], 1, accs[0], par2[0])
                for t in range(KT):
                    lru_tile(t // 2, t % 2, t // (KT // GROUPS))
                for n in range(3):
                    dve.wait_ge(roots, n + 1)
                    dve.reciprocal(tmp[2 + n][:], tmp[2 + n][:])


def last_half_step(nc, o, d, gate_up, down):
    with ExitStack() as ctx:
        def sem(name):
            return o.semaphore(nc, name)

        x = ctx.enter_context(nc.sbuf_tensor("x3", [P, KT, T], F32))
        h = [ctx.enter_context(nc.sbuf_tensor(f"h3_{n}", [P, KT, T], F32R)) for n in ("hi", "lo")]
        sets = [ctx.enter_context(nc.psum_tensor(f"set3_{s}", [P, CHUNKS, 512], F32)) for s in range(2)]
        weights = Weights(nc, ctx, o, "c")
        norm2 = Norm(nc, sem, "ffn2", x, o.tmp, o.tmp[2], o.tmp[3], o.ones, o.vecs, sets[0], o.eps)
        last_norm = Norm(nc, sem, "final", x, o.tmp, o.tmp[2], o.tmp[3], o.ones, o.vecs, sets[0], o.eps)
        ffn = Ffn(sem, "ffn2", weights, x, o.xn, h, o.tmp, sets)
        ssd_landed = [sem(f"ssd_tile_landed{k}") for k in range(KT)]
        lru_landed = [sem(f"lru_tile_landed{n}") for n in range(2)]
        x_landed = [sem(f"x3_tile_landed{k}") for k in range(KT)]
        ssd_split, lru_split = sem("ssd_tile_split"), sem("lru_tile_split")
        ssd_scaled, ssd_high = sem("ssd_tile_scaled"), sem("ssd_tile_high_part")
        projections = KT
        reads = projections + sum(n for _, n in FFN_BLOCKS) + KT // 2 * len(FFN_BLOCKS)

        with nc.Block() as block:
            @block.sync
            def _(sp):
                units = Units()
                for k in range(KT):
                    sp.dma_start(x[:, k, :], d.mixed[KT + k]).then_inc(ssd_landed[k], 16)
                for half in (1, 0):
                    def load(i):
                        for s in range(2):
                            weights.load(sp, units, i, s, d.w_out[i * 2 + s, :, half * KT * P:(half + 1) * KT * P], KT)
                    first_then_loop(sp, KT // 2, load)
                    units.n += KT
                ffn.sync(sp, units, gate_up, down)
                for k in range(KT):
                    sp.wait_ge(last_norm.done, k + 1)
                    sp.dma_start(d.y_out[:, k, :], o.tmp[k % 2][:]).then_inc(last_norm.stored[k % 2], 16)
                for n in range(2):
                    sp.wait_ge(last_norm.stored[n], 16 * KT // 2)

            @block.gpsimd
            def _(pool):
                units = Units()
                for half in range(2):
                    def split_pair(i):
                        for s in range(2):
                            weights.split_unit(pool, units, i, s, KT)
                    first_then_loop(pool, KT // 2, split_pair)
                    units.n += KT
                ffn.pool(pool, units)

            @block.scalar
            def _(act):
                high_parts(act, o.tmp, o.xn[0], ssd_scaled, ssd_high)
                for k in range(2):
                    act.wait_ge(ssd_split, 6 + k + 1)
                    act.dma_start(o.tmp[k][:], d.mixed[k]).then_inc(lru_landed[k], 16)
                for k in range(KT):
                    act.wait_ge(ssd_landed[k], 16)
                    act.dma_start(x[:, k, :], d.x_kept[:, k, :]).then_inc(x_landed[k], 16)
                for k in range(2, KT):
                    act.wait_ge(lru_split, k - 1)
                    act.dma_start(o.tmp[k % 2][:], d.mixed[k]).then_inc(lru_landed[k % 2], 16)
                units = Units()
                units.n += 2 * KT
                for s in range(2):
                    act.wait_ge(ffn.set_read[s], projections)
                norm2.scalar(act, o.xn[0])
                ffn.scalar(act, units)
                for s in range(2):
                    act.wait_ge(ffn.set_read[s], reads)
                last_norm.scalar(act)

            @block.tensor
            def _(pe):
                units = Units()
                x_hi, x_lo = o.xn
                for half in (1, 0):
                    hi, lo = o.xn if half else h

                    def project(i):
                        for s in range(2):
                            ffn.wait_set(pe, units, i, s)
                            ready = None
                            if half and isinstance(i, int) and s == 0:
                                def ready(k):
                                    pe.wait_ge(ssd_split, k + 1)
                            weights.products(pe, units, i, s, sets[s], hi, lo, KT, ready=ready)
                    if not half:
                        pe.wait_ge(lru_split, KT)
                    first_then_loop(pe, KT // 2, project)
                    units.n += KT
                norm2.tensor(pe)
                pe.wait_ge(norm2.rooted, 1)
                ffn.tensor(pe, units, norm2.done)
                last_norm.tensor(pe)

            @block.vector
            def _(dve):
                units = Units()
                for k in range(KT):
                    dve.drain()
                    dve.wait_ge(ssd_landed[k], 16)
                    dve.scalar_tensor_tensor(o.tmp[k % 2][:], x[:, k, :], o.vecs[:, V_SSD + k:V_SSD + k + 1],
                                             o.tmp[3 + k // 4][:], ALU.mult, ALU.mult).then_inc(ssd_scaled, 1)
                    if k:
                        low_part(dve, o.tmp, *o.xn, k - 1, ssd_high, ssd_split)
                low_part(dve, o.tmp, *o.xn, KT - 1, ssd_high, ssd_split)
                for k in range(KT):
                    dve.wait_ge(weights.used, k + 1)
                    dve.wait_ge(x_landed[k], 16)
                    tile = cut(x[:, k, :])
                    dve.scalar_tensor_tensor(tile, whole(sets[k % 2]), 1.0, tile, ALU.mult, ALU.add).then_inc(ffn.set_read[k % 2], 1)
                    lru = o.tmp[k % 2]
                    dve.wait_ge(lru_landed[k % 2], 16 * (k // 2 + 1))
                    dve.scalar_tensor_tensor(lru[:], lru[:], o.vecs[:, V_LRU + k:V_LRU + k + 1], o.tmp[2][:], ALU.mult, ALU.mult)
                    dve.drain()
                    split_rows(dve, lru, h[0][:, k, :], h[1][:, k, :]).then_inc(lru_split, 1)
                units.n += KT
                ffn.residual(dve, units, 1.0)
                norm2.vector(dve, V_FFN2, *o.xn)
                ffn.vector(dve, units)
                last_norm.vector(dve, V_FINAL)


class Names:
    pass


def build(nc, ins, outs):
    d = Names()
    (xt, vecs, gate_up1, down1, w_in, w_dt, pars, hist, heads, lru_h0, state_in, gates, w_out, gate_up2, down2) = ins
    d.y_out, d.tail_out, d.kept_out, d.lru_h_out, d.prompt_state, d.state_out = outs
    d.w_in, d.w_dt, d.pars, d.hist, d.heads, d.lru_h0, d.state_in, d.gates, d.w_out = (
        w_in, w_dt, pars, hist, heads, lru_h0, state_in, gates, w_out)
    d.x_kept = nc.dram_tensor("x_kept", [P, KT, T], F32, kind="Internal").ap()
    d.silu_z = nc.dram_tensor("silu_z", [KT, P, T], F32, kind="Internal").ap()
    d.gelu_y = nc.dram_tensor("gelu_y", [KT, P, T], F32, kind="Internal").ap()
    d.mixed = nc.dram_tensor("mixed", [2 * KT, P, T], F32, kind="Internal").ap()
    with ExitStack() as ctx:
        def sb(name, shape, dt=F32):
            return ctx.enter_context(nc.sbuf_tensor(name, shape, dt))

        o = Names()
        o.semaphores = []

        def semaphore(nc, name):
            o.semaphores.append(nc.alloc_semaphore(name=name))
            return o.semaphores[-1]
        o.semaphore = semaphore

        def end_of_block():
            nc.all_engine_barrier()
            nc.clear_and_free_semaphores(o.semaphores)
            nc.all_engine_barrier()
            o.semaphores = []
        o.vecs_dram = vecs
        o.vecs, o.ones, o.eps = sb("vecs", [P, V_COLS]), sb("ones", [P, P]), sb("eps", [P, 1])
        o.xn = [sb(f"xn_{n}", [P, KT, T], F32R) for n in ("hi", "lo")]
        o.tmp = [sb(f"tmp{n}", [P, T]) for n in range(5)]
        first_half_step(nc, o, xt, gate_up1, down1, d.x_kept)
        end_of_block()
        mixer(nc, o, d)
        end_of_block()
        last_half_step(nc, o, d, gate_up2, down2)


def kernel(x_prompt, x_sample, state_lru_conv, state_lru_h, state_ssd_conv, state_ssd_h,
           ffn1_norm, ffn1_w_gate, ffn1_w_up, ffn1_w_down, mix_norm, w_in,
           lru_conv_w, lru_conv_b, lru_gate_a_w, lru_gate_a_b, lru_gate_x_w, lru_gate_x_b,
           lru_lambda, lru_out_norm, ssd_conv_w, ssd_conv_b, ssd_dt_bias, ssd_a_log, ssd_d,
           ssd_norm, w_out, ffn2_norm, ffn2_w_gate, ffn2_w_up, ffn2_w_down, final_norm):
    import numpy as np
    import concourse.bacc as bacc
    from concourse.bass_utils import run_bass_kernel_spmd

    def features(v):
        v = np.asarray(v)
        v = v.reshape(v.shape[:-1] + (v.shape[-1] // P, P))
        return np.moveaxis(np.moveaxis(v, -1, 0), -1, 1)

    def tiles(w, order=None):
        w = np.asarray(w)
        k, m = w.shape[0] // P, w.shape[1] // P
        w = w.reshape(k, P, m, P).transpose(2, 1, 0, 3)
        if order is not None:
            w = w[order]
        return w.reshape(-1, P, k * P)

    def gate_up(gate, up):
        return np.stack([tiles(gate), tiles(up)], 1).reshape(2 * FT, P, DM)

    x = np.concatenate([np.asarray(x_prompt)[0], np.asarray(x_sample)[:, 0]])
    order = [32, 33, 34, 35] + list(range(24, 32)) + [n + 8 * z for n in range(8) for z in (2, 1)] + list(range(8))
    w_in0 = np.asarray(w_in)[0]
    xbc_order = [8, 9, 10, 11] + list(range(8))
    conv_w = np.concatenate([features(ssd_conv_w[0])[:, xbc_order], features(lru_conv_w[0])], 1)
    conv_b = np.concatenate([features(ssd_conv_b[0])[:, xbc_order], features(lru_conv_b[0])], 1)
    pars = np.zeros((P, CT, PARS), np.float32)
    pars[:, :, 0:TAPS] = conv_w
    pars[:, :, PAR_BIAS] = conv_b
    pars[:, XT:, PAR_GA] = features(lru_gate_a_b[0])
    pars[:, XT:, PAR_GX] = features(lru_gate_x_b[0])
    pars[:, XT:, PAR_LAM] = features(lru_lambda[0])
    rows_ssd = features(state_ssd_conv[0])[:, xbc_order]
    hist = np.concatenate([rows_ssd, features(state_lru_conv[0])], 1)
    hist_in = hist.transpose(0, 1, 3, 2).reshape(P, CT, HIST * DEC)
    gates = np.zeros((KT, 2, P, P), np.float32)
    for n, g in enumerate((lru_gate_a_w, lru_gate_x_w)):
        g = np.asarray(g)[0].reshape(KT, 2, HD, HD)
        gates[:, n, 0:HD, 0:HD] = g[:, 0]
        gates[:, n, HD:P, HD:P] = g[:, 1]
    gates = gates.reshape(KT // 2, 2, 2, P, P).transpose(0, 3, 1, 2, 4).reshape(KT // 2, P, 4 * P)
    d_rows = np.broadcast_to(np.asarray(ssd_d)[0][:, None], (HEADS, HD)).reshape(DM)
    vecs = np.concatenate([features(v) for v in (ffn1_norm[0], mix_norm[0], ffn2_norm[0], final_norm,
                                                 lru_out_norm[0], ssd_norm[0], d_rows)], 1)
    state = np.asarray(state_ssd_h)[0].reshape(DEC, KT, P, NST).transpose(1, 2, 0, 3)
    ins = {
        "xt": features(x),
        "vecs": vecs,
        "gate_up1": gate_up(ffn1_w_gate[0], ffn1_w_up[0]),
        "down1": tiles(ffn1_w_down[0]),
        "w_in": tiles(w_in0[:, 0:36 * P], order),
        "w_dt": w_in0[:, 36 * P:].reshape(KT, P, HEADS).transpose(1, 0, 2).reshape(P, KT * HEADS),
        "pars": pars,
        "hist": hist_in,
        "heads": np.stack([np.asarray(ssd_dt_bias)[0], np.asarray(ssd_a_log)[0]], 1),
        "lru_h0": features(state_lru_h[0]),
        "state_in": state,
        "gates": gates,
        "w_out": tiles(w_out[0]),
        "gate_up2": gate_up(ffn2_w_gate[0], ffn2_w_up[0]),
        "down2": tiles(ffn2_w_down[0]),
    }
    outs = {"y": [P, KT, T], "tail": [P, CT, HIST + DEC], "kept": [P, CT, (HIST - 1) * DEC],
            "lru_h": [P, KT, 1 + DEC],
            "prompt_state": [P, DM], "state_out": [KT, P, DEC, NST]}
    ins = {f"in_{n}": np.ascontiguousarray(a) for n, a in ins.items()}
    nc = bacc.Bacc("TRN2", target_bir_lowering=False, num_devices=1, dynamic_dma_scratch_size=1024)
    in_aps = [nc.dram_tensor(n, a.shape, mybir.dt.from_np(a.dtype), kind="ExternalInput").ap() for n, a in ins.items()]
    out_aps = [nc.dram_tensor(f"out_{n}", s, F32, kind="ExternalOutput").ap() for n, s in outs.items()]
    build(nc, in_aps, out_aps)
    r = run_bass_kernel_spmd(nc, [ins], core_ids=[0]).results[0]
    y, tail, kept, lru_h, prompt_state, state_out = (np.asarray(r[f"out_{n}"]) for n in outs)

    def rows(v):
        v = np.moveaxis(np.moveaxis(v, 0, -1), 0, -2)
        return v.reshape(v.shape[:-2] + (-1,))

    y = rows(y)
    inverse = [xbc_order.index(n) for n in range(XT)]
    ssd_tail, lru_tail = tail[:, inverse], tail[:, XT:]
    kept = kept.reshape(P, CT, HIST - 1, DEC)
    ssd_kept, lru_kept = kept[:, inverse], kept[:, XT:]

    def conv_states(tail, kept):
        prompt = rows(tail[:, :, 0:HIST])
        kept = rows(kept).swapaxes(0, 1)
        return prompt[None, None], np.concatenate([kept, rows(tail[:, :, HIST:])[:, None]], 1)[None]

    p_lru_conv, s_lru_conv = conv_states(lru_tail, lru_kept)
    p_ssd_conv, s_ssd_conv = conv_states(ssd_tail, ssd_kept)
    h_rows = rows(lru_h)
    p_state = prompt_state.reshape(NST, HEADS, HD).transpose(1, 2, 0)
    s_state = state_out.transpose(2, 0, 1, 3).reshape(DEC, HEADS, HD, NST)
    c = np.ascontiguousarray
    return (c(y[None, 0:PROMPT]), c(y[PROMPT:, None]),
            c(p_lru_conv), c(h_rows[None, 0:1]), c(p_ssd_conv), c(p_state[None, None]),
            c(s_lru_conv), c(h_rows[None, 1:]), c(s_ssd_conv), c(s_state[None]))
```
